# Optimizing a Trainium2 kernel written in Bass

```python
import jax, jax.numpy as jnp
from jax import lax
import numpy as np

D_MODEL = 1024
BATCH = 1
SEQ = 1024
DEPTH = 1
DEC_BATCH = 8
DEC_SEQ = 1
PAST_LEN = 4096
PAGE_SIZE = 128

ATTN_WIDTH = D_MODEL // 2
POOL_WIDTH = D_MODEL - ATTN_WIDTH
N_HEADS = 8
HEAD_DIM = ATTN_WIDTH // N_HEADS
POOL_WINDOWS = (2, 4, 8, 16)
N_POOL_GROUPS = len(POOL_WINDOWS)
POOL_GROUP_DIM = POOL_WIDTH // N_POOL_GROUPS
POOL_STATE_LEN = max(POOL_WINDOWS) - 1
D_FF = -(-8 * D_MODEL // 768) * 256
IN_COLS = 3 * ATTN_WIDTH + N_HEADS + POOL_WIDTH
QBLOCK = 128
DEEPNORM_ALPHA = (2.0 * DEPTH) ** 0.25
DEEPNORM_BETA = (8.0 * DEPTH) ** -0.25
LN_EPS = 1e-5
NEG_INF = -1e30

kernel_name = "hymba_fox_poolformer_deepnorm_step"

def layer_norm(x, g, b):
    xf = x.astype(jnp.float32)
    mu = jnp.mean(xf, axis=-1, keepdims=True)
    var = jnp.mean(jnp.square(xf - mu), axis=-1, keepdims=True)
    return ((xf - mu) * lax.rsqrt(var + LN_EPS) * g + b).astype(x.dtype)

def project(x, w_in, b_f):
    h = jnp.einsum('bsd,dc->bsc', x, w_in)
    B, S = h.shape[:2]
    A = ATTN_WIDTH
    q = h[..., :A].reshape(B, S, N_HEADS, HEAD_DIM)
    k = h[..., A:2 * A].reshape(B, S, N_HEADS, HEAD_DIM)
    v = h[..., 2 * A:3 * A].reshape(B, S, N_HEADS, HEAD_DIM)
    logf = jax.nn.log_sigmoid((h[..., 3 * A:3 * A + N_HEADS] + b_f).astype(jnp.float32))
    u = h[..., 3 * A + N_HEADS:]
    return q, k, v, logf, u

def pool_mix(u_ext, start_pos, w_pool, pool_scale):
    B, L, _ = u_ext.shape
    n_new = L - POOL_STATE_LEN
    c = jnp.pad(jnp.cumsum(u_ext.astype(jnp.float32), axis=1), ((0, 0), (1, 0), (0, 0)))
    end = c[:, POOL_STATE_LEN + 1:]
    pos = start_pos + jnp.arange(n_new)
    means = []
    for g, w in enumerate(POOL_WINDOWS):
        lo, hi = g * POOL_GROUP_DIM, (g + 1) * POOL_GROUP_DIM
        begin = c[:, POOL_STATE_LEN + 1 - w:POOL_STATE_LEN + 1 - w + n_new, lo:hi]
        cnt = jnp.minimum(pos + 1, w).astype(jnp.float32)[None, :, None]
        means.append((end[..., lo:hi] - begin) / cnt)
    mean = jnp.concatenate(means, axis=-1)
    d = (mean - u_ext[:, POOL_STATE_LEN:].astype(jnp.float32)).astype(u_ext.dtype)
    d = d.reshape(B, n_new, N_POOL_GROUPS, POOL_GROUP_DIM)
    out = jnp.einsum('bsgc,gcd->bsgd', d, w_pool).reshape(B, n_new, POOL_WIDTH)
    return out * pool_scale

def fox_prompt(q, k, v, logf):
    B, S = q.shape[:2]
    Fh = jnp.cumsum(logf, axis=1).transpose(0, 2, 1)
    scale = HEAD_DIM ** -0.5
    kpos = jnp.arange(S)

    def block(i):
        q_blk = lax.dynamic_slice_in_dim(q, i * QBLOCK, QBLOCK, axis=1)
        F_blk = lax.dynamic_slice_in_dim(Fh, i * QBLOCK, QBLOCK, axis=2)
        s = jnp.einsum('bqhd,bkhd->bhqk', q_blk, k, preferred_element_type=jnp.float32) * scale
        s = s + (F_blk[..., :, None] - Fh[..., None, :])
        qpos = i * QBLOCK + jnp.arange(QBLOCK)
        s = jnp.where(kpos[None, :] <= qpos[:, None], s, NEG_INF)
        p = jax.nn.softmax(s, axis=-1)
        return jnp.einsum('bhqk,bkhd->bqhd', p.astype(v.dtype), v)

    out = lax.map(block, jnp.arange(S // QBLOCK))
    return out.transpose(1, 0, 2, 3, 4).reshape(B, S, ATTN_WIDTH)

def fox_sample(q, k_new, v_new, logf_new, cache_k, cache_v, cache_logf, page_table):
    DB, DS = q.shape[:2]
    P = page_table.shape[1] * PAGE_SIZE
    k_past = cache_k[page_table].reshape(DB, P, N_HEADS, HEAD_DIM)
    v_past = cache_v[page_table].reshape(DB, P, N_HEADS, HEAD_DIM)
    f_past = cache_logf[page_table].reshape(DB, P, N_HEADS).astype(jnp.float32)
    k_all = jnp.concatenate([k_past, k_new.astype(k_past.dtype)], axis=1)
    v_all = jnp.concatenate([v_past, v_new.astype(v_past.dtype)], axis=1)
    Fh = jnp.cumsum(jnp.concatenate([f_past, logf_new], axis=1), axis=1).transpose(0, 2, 1)
    s = jnp.einsum('bqhd,bkhd->bhqk', q, k_all, preferred_element_type=jnp.float32) * HEAD_DIM ** -0.5
    s = s + (Fh[..., P:, None] - Fh[..., None, :])
    kpos = jnp.arange(P + DS)
    qpos = P + jnp.arange(DS)
    s = jnp.where(kpos[None, :] <= qpos[:, None], s, NEG_INF)
    p = jax.nn.softmax(s, axis=-1)
    out = jnp.einsum('bhqk,bkhd->bqhd', p.astype(v_all.dtype), v_all)
    return out.reshape(DB, DS, ATTN_WIDTH)

def finish(x, attn, pool, w_o, ln1_g, ln1_b, w_gate, w_up, w_down, ln2_g, ln2_b):
    mix = jnp.einsum('bsc,cd->bsd', jnp.concatenate([attn.astype(x.dtype), pool.astype(x.dtype)], axis=-1), w_o)
    x1 = layer_norm(DEEPNORM_ALPHA * x + mix, ln1_g, ln1_b)
    hid = jax.nn.silu(jnp.einsum('bsd,df->bsf', x1, w_gate)) * jnp.einsum('bsd,df->bsf', x1, w_up)
    ffn = jnp.einsum('bsf,fd->bsd', hid, w_down)
    return layer_norm(DEEPNORM_ALPHA * x1 + ffn, ln2_g, ln2_b)

def setup_inputs(seed: int = 0) -> dict:
    key = jax.random.key(seed)
    ks = jax.random.split(key, 24)
    f32 = jnp.float32
    n_pages = PAST_LEN // PAGE_SIZE
    n_used = DEC_BATCH * n_pages
    n_pool = n_used + n_used // 4
    x_prompt = jax.random.normal(ks[0], (BATCH, SEQ, D_MODEL), f32)
    x_sample = jax.random.normal(ks[1], (DEC_BATCH, DEC_SEQ, D_MODEL), f32)
    cache_k = jax.random.normal(ks[2], (DEPTH, n_pool, PAGE_SIZE, N_HEADS, HEAD_DIM), f32)
    cache_v = DEEPNORM_BETA * jax.random.normal(ks[3], (DEPTH, n_pool, PAGE_SIZE, N_HEADS, HEAD_DIM), f32)
    cache_logf = jax.nn.log_sigmoid(3.0 + 0.5 * jax.random.normal(ks[4], (DEPTH, n_pool, PAGE_SIZE, N_HEADS), f32))
    state_pool = jax.random.normal(ks[5], (DEPTH, DEC_BATCH, POOL_STATE_LEN, POOL_WIDTH), f32)
    page_table = jax.random.permutation(ks[6], n_pool)[:n_used].reshape(DEC_BATCH, n_pages).astype(jnp.int32)
    col_scale = jnp.concatenate([
        jnp.ones((2 * ATTN_WIDTH,), f32),
        jnp.full((ATTN_WIDTH,), DEEPNORM_BETA, f32),
        jnp.full((N_HEADS,), 0.1, f32),
        jnp.ones((POOL_WIDTH,), f32)])
    w_in = jax.random.normal(ks[7], (DEPTH, D_MODEL, IN_COLS), f32) * D_MODEL ** -0.5 * col_scale
    b_f = 3.0 + 0.5 * jax.random.normal(ks[8], (DEPTH, N_HEADS), f32)
    w_pool = jax.random.normal(ks[9], (DEPTH, N_POOL_GROUPS, POOL_GROUP_DIM, POOL_GROUP_DIM), f32) * POOL_GROUP_DIM ** -0.5
    pool_scale = 1.0 + 0.1 * jax.random.normal(ks[10], (DEPTH, POOL_WIDTH), f32)
    w_o = jax.random.normal(ks[11], (DEPTH, D_MODEL, D_MODEL), f32) * D_MODEL ** -0.5 * DEEPNORM_BETA
    ln1_g = 1.0 + 0.1 * jax.random.normal(ks[12], (DEPTH, D_MODEL), f32)
    ln1_b = 0.02 * jax.random.normal(ks[13], (DEPTH, D_MODEL), f32)
    w_gate = jax.random.normal(ks[14], (DEPTH, D_MODEL, D_FF), f32) * D_MODEL ** -0.5
    w_up = jax.random.normal(ks[15], (DEPTH, D_MODEL, D_FF), f32) * D_MODEL ** -0.5
    w_down = jax.random.normal(ks[16], (DEPTH, D_FF, D_MODEL), f32) * D_FF ** -0.5 * DEEPNORM_BETA
    ln2_g = 1.0 + 0.1 * jax.random.normal(ks[17], (DEPTH, D_MODEL), f32)
    ln2_b = 0.02 * jax.random.normal(ks[18], (DEPTH, D_MODEL), f32)
    return {"x_prompt": x_prompt, "x_sample": x_sample, "cache_k": cache_k, "cache_v": cache_v,
            "cache_logf": cache_logf, "state_pool": state_pool, "page_table": page_table,
            "w_in": w_in, "b_f": b_f, "w_pool": w_pool, "pool_scale": pool_scale, "w_o": w_o,
            "ln1_g": ln1_g, "ln1_b": ln1_b, "w_gate": w_gate, "w_up": w_up, "w_down": w_down,
            "ln2_g": ln2_g, "ln2_b": ln2_b}

def reference(x_prompt, x_sample, cache_k, cache_v, cache_logf, state_pool, page_table,
              w_in, b_f, w_pool, pool_scale, w_o, ln1_g, ln1_b, w_gate, w_up, w_down, ln2_g, ln2_b):
    xp, xs = x_prompt, x_sample
    kp, vp, fp, pp, ksm, vsm, fsm, psm = [], [], [], [], [], [], [], []
    for l in range(DEPTH):
        q, k, v, logf, u = project(xp, w_in[l], b_f[l])
        attn = fox_prompt(q, k, v, logf)
        u_ext = jnp.pad(u, ((0, 0), (POOL_STATE_LEN, 0), (0, 0)))
        pool = pool_mix(u_ext, 0, w_pool[l], pool_scale[l])
        kp.append(k)
        vp.append(v)
        fp.append(logf.astype(xp.dtype))
        pp.append(u_ext[:, -POOL_STATE_LEN:])
        xp = finish(xp, attn, pool, w_o[l], ln1_g[l], ln1_b[l], w_gate[l], w_up[l], w_down[l], ln2_g[l], ln2_b[l])
        q, k, v, logf, u = project(xs, w_in[l], b_f[l])
        attn = fox_sample(q, k, v, logf, cache_k[l], cache_v[l], cache_logf[l], page_table)
        u_ext = jnp.concatenate([state_pool[l].astype(u.dtype), u], axis=1)
        pool = pool_mix(u_ext, PAST_LEN, w_pool[l], pool_scale[l])
        ksm.append(k)
        vsm.append(v)
        fsm.append(logf.astype(xs.dtype))
        psm.append(u_ext[:, -POOL_STATE_LEN:])
        xs = finish(xs, attn, pool, w_o[l], ln1_g[l], ln1_b[l], w_gate[l], w_up[l], w_down[l], ln2_g[l], ln2_b[l])
    return (xp, xs, jnp.stack(kp), jnp.stack(vp), jnp.stack(fp), jnp.stack(pp),
            jnp.stack(ksm), jnp.stack(vsm), jnp.stack(fsm), jnp.stack(psm))


_drawn_inputs = setup_inputs


def setup_inputs(seed=0):
    import zlib

    import numpy as np

    out = dict(_drawn_inputs(seed))
    spreads = {}
    factors = {'cache_logf': 33.094, 'ln2_b': 2.923}
    for name, (base, spread) in spreads.items():
        noise = np.random.default_rng([zlib.crc32(name.encode()), seed]).standard_normal(out[name].shape)
        drawn = base * np.exp(spread * noise) if base else spread * noise
        out[name] = __import__('jax').numpy.asarray(drawn.astype(out[name].dtype))
    for name, factor in factors.items():
        out[name] = (out[name] * factor).astype(out[name].dtype)
    return out
```

```python
from contextlib import ExitStack

import numpy as np

import concourse.bass as bass
from concourse import mybir

F32 = mybir.dt.float32
F32R = mybir.dt.float32r
I32 = mybir.dt.int32
U32 = mybir.dt.uint32
ALU = mybir.AluOpType
ACT = mybir.ActivationFunctionType
AX = mybir.AxisListType

P = 128
D = 1024
KC = D // P
ROWS = 1024
RT = ROWS // P
NB = 8
H = 8
HD = 64
AW = H * HD
PAIRS = H // 2
STEPS = 2 * RT
GROUPS = 4
STATE = 15
NPAGE = 32
CH = 4
NCH = NPAGE // CH
POOL_PAGES = 320
DFF = 2816
FT = DFF // P
SCALE = HD ** -0.5
ALPHA = 2.0 ** 0.25
EPS = 1e-5
NEG = -1e30
HALF = 512
NWT = 3 * PAIRS + GROUPS
WS = 3
OC = 4
OCW = D // OC
NITER = (FT - 1) // 3
VALUES_AFTER = {1: (0,), 2: (1,), 3: (2,), 4: (3,), 5: (4,), 6: (5,), 7: (6, 7)}


class Chain:

    def __init__(self, eng, sem):
        self.eng, self.sem, self.n, self.base = eng, sem, 0, 0

    def __call__(self, ins):
        self.n += 1
        ins.then_inc(self.sem, 1)
        self.eng.wait_ge(self.sem, self.base + self.n)

    def iteration(self, i, per):
        self.before, self.per = self.n, per
        self.base, self.n = i * per + self.n, 0

    def after(self, times):
        assert self.n == self.per, (self.n, self.per)
        self.base, self.n = 0, self.before + self.per * times


def numbered(names):
    return {name: n for n, name in enumerate(names)}


def build(nc, t):
    ctx = ExitStack()
    with ctx:
        def sb(name, shape, dt=F32):
            return ctx.enter_context(nc.sbuf_tensor(name, shape, dt))

        def sem(name):
            return ctx.enter_context(nc.semaphore(name))

        XH = sb("XH", [P, KC, ROWS], F32R)
        XL = sb("XL", [P, KC, ROWS], F32R)
        WR = sb("WR", [P, WS, D])
        WH = sb("WH", [P, WS, D], F32R)
        WL = sb("WL", [P, WS, D], F32R)
        R2 = sb("R2", [P, 6, D], F32R)
        ACC = sb("ACC", [P, RT, D])
        AR = sb("AR", [P, 10 * D])
        ident = sb("ident_sb", [P, P])
        identR = sb("identR", [P, P], F32R)
        causalR = sb("causalR", [P, P], F32R)
        blkmask = sb("blkmask_sb", [P, H])
        QB = sb("QB", [P, AW])
        SC = sb("SC", [P, NPAGE, H])
        PR = sb("PR", [P, NPAGE, H])
        GB = sb("GB", [P, NPAGE, H])
        PD = sb("PD", [P, 4, 32])
        PND = sb("PND", [P, 4, 32])
        PN = sb("PN", [P, H])
        psum_row = sb("psum_row", [P, H])
        xsH = sb("xsH", [P, KC, NB], F32R)
        xsL = sb("xsL", [P, KC, NB], F32R)
        wfH = sb("wfH", [P, KC, H], F32R)
        wfL = sb("wfL", [P, KC, H], F32R)
        bfc = sb("bfc", [H, 1])
        psc = sb("psc", [P, GROUPS])
        ones = sb("ones", [P, P])
        CS = sb("CS", [P, KC, NB])
        LNEW = sb("LNEW", [NB, NB, H])
        lsub = sb("lsub", [NB, H])
        negm = sb("negm", [P, 2])
        rsum = sb("rsum", [P, 2])
        rinv = sb("rinv", [P, 2])
        mxp = sb("mxp", [P, H])
        Mb = sb("Mb", [P, H])
        gm = sb("gm", [H, 1])
        dg = sb("dg", [H, H])
        rden = sb("rden", [P, 1])
        st = sb("st", [P, 2, 6])
        mv = sb("mv", [P, RT + 1, 2])
        sd = sb("sd", [P, RT + 1, 2])
        rs = sb("rs", [P, RT + 1, 2])
        page = sb("page_sb", [1, NB * NPAGE], I32)
        page_row = sb("page_row_sb", [P, 2], I32)
        snew = sb("snew", [NB, H])
        suftot = sb("suftot", [P, 2, H])
        PSM = ctx.enter_context(nc.psum_tensor("PSM", [P, 8, HALF], F32))

        negF_d = nc.dram_tensor("negF_d", (H, ROWS), F32).ap()
        q_d = nc.dram_tensor("q_d", (NB, AW), F32).ap()
        G_d = nc.dram_tensor("G_d", (NB, P, NPAGE * H), F32).ap()

        def pb(u):
            return PSM[:, 2 * (u % 2):2 * (u % 2) + 2, :].rearrange("p a n -> p (a n)")

        TB = PSM[:, 4:6, :].rearrange("p a n -> p (a n)")
        OB = PSM[:, 6, :]
        B7 = PSM[:, 7, :]

        causal = GB[:].rearrange("p t h -> p (t h)")[:, 0:P]
        xs_raw = SC[:].rearrange("p t h -> p (t h)")[:, 0:KC * NB]
        wf_raw = SC[:].rearrange("p t h -> p (t h)")[:, KC * NB:KC * (NB + H)]
        f_rows = PR[:, 0:RT + 1, :]
        nmask = PR[0:NB, 16:16 + NB, :]
        L = [AR[:, n * D:(n + 1) * D] for n in (0, 1)]
        PT = [AR[:, n * D:(n + 1) * D] for n in (2, 3)]
        NF = [AR[:, n * D:(n + 1) * D] for n in (4, 5)]
        KST = AR[:, 6 * D:7 * D]
        VST = AR[:, 7 * D:8 * D]
        KN = AR[:, 8 * D:9 * D]
        VN = AR[:, 9 * D:10 * D]
        FRW = ROWS + NB
        fz, fa, fb, fnf = (AR[0:H, n * 1040:n * 1040 + FRW] for n in range(4))
        fone = AR[0:H, 4160:4160 + ROWS]
        LF, LS = ACC[:, 0:2, :], ACC[:, 2:4, :]
        GT = ACC[:, 4:6, :]
        scanmask = ACC[:, 6, :]
        cum = ACC[:, 7, 0:P]
        UW = ROWS + 16
        UB = [AR[:, n * UW:(n + 1) * UW] for n in range(3)]
        DB = AR[:, 3 * UW:3 * UW + ROWS]
        SN = AR[0:NB, 4160:4160 + NWT * P]
        at = 6 * D + 128
        UN = AR[0:STATE, at:at + AW]
        PROD = AR[0:NB, 7 * D:7 * D + AW]
        WP = AR[:, 7 * D + AW:8 * D].rearrange("p (g n) -> p g n", g=GROUPS)
        STT = AR[0:NB * STATE, 8 * D:8 * D + AW]
        RC = AR[:, 8 * D + 512:8 * D + 576].rearrange("p (g n) -> p g n", g=GROUPS)
        SEL = AR[0:NB * STATE, 8 * D + 576:8 * D + 608].rearrange("p (g n) -> p g n", g=GROUPS)
        SS = AR[:, 8 * D + 608:8 * D + 640].rearrange("p (g n) -> p g n", g=GROUPS)
        SD = AR[:, 8 * D + 640:8 * D + 672].rearrange("p (g n) -> p g n", g=GROUPS)
        SST = AR[:, 8 * D + 672:8 * D + 800].rearrange("p (j b) -> p j b", b=NB)
        KR = [AR[:, n * 2 * D:(n + 1) * 2 * D] for n in (0, 1)]
        VR = [AR[:, n * 2 * D:(n + 1) * 2 * D] for n in (2, 3)]
        LG, LB = AR[:, 8 * D:9 * D], AR[:, 9 * D:10 * D]
        GU = AR[:, 8 * D:9 * D]
        AM = AR[:, 9 * D:9 * D + AW]
        VS = AR[:, 9 * D + AW:10 * D]
        LG2, LB2 = WR[:, 0, :], WR[:, 1, :]
        TR = [AR[:, n * D:(n + 1) * D] for n in range(6)]
        xs1, xs2 = AR[0:NB, 6 * D:7 * D], AR[0:NB, 7 * D:8 * D]
        sg, sbeta = AR[0:NB, 8 * D:9 * D], AR[0:NB, 9 * D:10 * D]
        hsilu = SC[:, 0:2, :]
        hid = SC[:, 2:4, :]

        order = ["F"]
        for p in range(PAIRS):
            order += [("q", p), ("k", p), ("v", p)] + [("s", p, s) for s in range(STEPS)]
        order += [("u", 0), ("u", 1), ("w", 0), ("u", 2), ("w", 1), ("u", 3), ("w", 2), ("w", 3), ("sn", 0), ("sn", 1)]
        order += [("o", c, i) for c in range(OC) for i in range(RT)]
        U = numbered(order)
        torder = [("g", 0), ("g", 1)]
        for p in range(PAIRS):
            torder += [("kn", p), ("vn", p)] + [("t", p, s) for s in range(STEPS)] + [("ct", p)]
        torder += [("un", g) for g in range(GROUPS)] + [("x1", i) for i in range(RT)]
        T = numbered(torder)
        oorder = ["fs", "ft", "c"]
        for p in range(PAIRS):
            oorder += [("pv", p, s) for s in range(STEPS)]
        O = numbered(oorder + ["sp", "sw"])
        tile_use = [U[(kind, p)] for p in range(PAIRS) for kind in "qkv"] + [U[("u", g)] for g in range(GROUPS)]

        xswf_ld, small_ld, raw_ld = sem("xswf_ld"), sem("small_ld"), [sem(f"raw_ld{n}") for n in range(WS)]
        consts, cons_hi = sem("consts"), sem("cons_hi")
        small_hi, small_lo = sem("small_hi"), sem("small_lo")
        ent_hi, ent_lo = sem("ent_hi"), sem("ent_lo")
        pb_full, pb_free = sem("pb_full"), sem("pb_free")
        tb_full, tb_free = sem("tb_full"), sem("tb_free")
        ob_full, ob_free = sem("ob_full"), sem("ob_free")
        dve_chain, pool_chain = sem("dve_chain"), sem("pool_chain")
        f_z, f_t, f_u, f_l, f_done = (sem("f_" + n) for n in ("z", "t", "u", "l", "done"))
        negF_st, g_st, misc_st = sem("negF_st"), sem("g_st"), sem("misc_st")
        nf_ld = [sem("nf_ld0"), sem("nf_ld1")]
        idx_ld, logf_ld = sem("idx_ld"), sem("logf_ld")
        suf_scan, q_hi, k_hi, kst_done = sem("suf_scan"), sem("q_hi"), sem("k_hi"), sem("kst_done")
        kn_st, vn_st, e_done, inv_done = sem("kn_st"), sem("vn_st"), sem("e_done"), sem("inv_done")
        pads, u_win, d_done = sem("pads"), sem("u_win"), sem("d_done")
        mix_ld, sst_done, sn_st = sem("mix_ld"), sem("sst_done"), sem("sn_st")
        sd_done, lnew_done = sem("sd_done"), sem("lnew_done")
        cat_hi, cat_lo = sem("cat_hi"), sem("cat_lo")
        wo_ld, wo_hi, wo_lo = sem("wo_ld"), sem("wo_hi"), sem("wo_lo")
        x_ld, ln1_ld, qb_ld, gb_ld, vs_ld, vs_zero = (sem(n) for n in ("x_ld", "ln1_ld", "qb_ld", "gb_ld", "vs_ld", "vs_zero"))
        n1_var, n1_sd, n1_rs, n1_y, n1_g, n1_b, x1_hi, x1_lo, n1_alpha = (
            sem("n1_" + n) for n in ("var", "sd", "rs", "y", "g", "b", "hi", "lo", "alpha"))
        ffn_ld = [sem(f"ffn_ld{n}") for n in range(WS)]
        ffn_hi = [sem(f"ffn_hi{n}") for n in range(WS)]
        ffn_lo = [sem(f"ffn_lo{n}") for n in range(WS)]
        g_full, u_full, d_full, d_free = sem("g_full"), sem("u_full"), sem("d_full"), sem("d_free")
        silu_done, gu_done, hh_done, hl_done = sem("silu_done"), sem("gu_done"), sem("hh_done"), sem("hl_done")
        k_ld = [sem("k_ld0"), sem("k_ld1")]
        v_ld = [sem("v_ld0"), sem("v_ld1")]
        k_mul, k_red, v_used, bank6_zero = sem("k_mul"), sem("k_red"), sem("v_used"), sem("bank6_zero")
        m_max, m_t, m_dg, m_b, m_sub, m_exp, m_sum, den_full, den_inv = (
            sem("m_" + n) for n in ("max", "t", "dg", "b", "sub", "exp", "sum", "den", "inv"))
        am_done, am_full, am_cs = sem("am_done"), sem("am_full"), sem("am_cs")
        ln2_ld, n2_var, n2_sd, n2_rs, n2_y, n2_g, n2_b, y_st = (
            sem("n2_" + n) for n in ("ld", "var", "sd", "rs", "y", "g", "b", "st"))
        t_ld, t_used = [sem(f"t_ld{n}") for n in range(6)], sem("t_used")
        e_ld, e_mix, e_var, e_sd, e_rs, e_x1, e_t, e_xt, e_vec_ld = (
            sem("e_" + n) for n in ("ld", "mix", "var", "sd", "rs", "x1", "t", "xt", "vec_ld"))
        e_silu, e_hid, e_y, e_st = (sem("e_" + n) for n in ("silu", "hid", "y", "st"))

        block = ctx.enter_context(nc.Block())

        @block.sync
        def _(sp):
            def pages(n, ring, slot, cache, done, used=None, count=None):
                numbers = [sp.value_load(page[0:1, bass.ds(n * CH + j, 1)], min_val=0, max_val=POOL_PAGES - 1)
                           for j in range(CH)]
                if used is not None:
                    sp.wait_ge(used, count)
                for j, p in enumerate(numbers):
                    sp.dma_start(ring[slot][:, j * AW:(j + 1) * AW],
                                 cache[bass.ds(p, 1), :, :].rearrange("a p n -> (a p) n")).then_inc(done[slot], 16)

            for dst, src in ((xs_raw, t["xsT"]), (wf_raw, t["wf"])):
                sp.dma_start(dst, src).then_inc(xswf_ld, 16)
            for e in range(KC + NWT):
                if e >= WS:
                    sp.wait_ge(ent_lo, e - WS + 1)
                sp.dma_start(WR[:, e % WS, :], t["xT"][:, e, :] if e < KC else t["w_in"][e - KC]
                             ).then_inc(raw_ld[e % WS], 16)
                if e == WS - 1:
                    for dst, src in ((bfc[:], t["bf"]), (scanmask, t["scanmask"]), (cum, t["cum"]),
                                     (ident[:], t["ident"]), (causal, t["causal"]), (psc[:], t["pscale"]),
                                     (page[:], t["page"]), (nmask, t["newmask"]), (blkmask[:], t["blkmask"])):
                        sp.dma_start(dst, src).then_inc(small_ld, 16)
                j = e - KC
                if j >= 2 and j % 3 == 2 and j // 3 < PAIRS:
                    p = j // 3
                    if p == 0:
                        sp.wait_ge(negF_st, 16)
                    for hh in range(2):
                        if p >= 1:
                            sp.wait_ge(pb_free, U[("s", p - 1, RT * hh + RT - 1)] + 1)
                        sp.dma_start(NF[hh], negF_d[2 * p + hh:2 * p + hh + 1, :].to_broadcast([P, ROWS])
                                     ).then_inc(nf_ld[hh], 16)
            sp.wait_ge(tb_free, T[("ct", PAIRS - 1)] + 1)
            sp.wait_ge(kn_st, 16 * PAIRS)
            for dst, src in ((WP, t["w_pool"]), (RC, t["rcnt"]), (SEL, t["sel"]), (STT, t["state"])):
                sp.dma_start(dst, src).then_inc(mix_ld, 16)

            sp.wait_ge(ent_lo, KC + NWT)
            for c in range(OC):
                if c >= 1:
                    sp.wait_ge(wo_lo, c)
                sp.dma_start(WR[:, 0:2, :].rearrange("p a n -> p (a n)"), t["w_o4"][c]).then_inc(wo_ld, 16)
                if c == 0:
                    sp.wait_ge(cat_lo, KC)
                    for i in range(RT):
                        sp.dma_start(ACC[:, i, :], t["x"][i * P:(i + 1) * P, :]).then_inc(x_ld, 16)
                    sp.wait_ge(sn_st, 16 * 4)
                    sp.wait_ge(vn_st, 16 * PAIRS)
                    sp.wait_ge(ob_free, O["sw"] + 1)
                    sp.dma_start(LG, t["ln1_g"].to_broadcast([P, D])).then_inc(ln1_ld, 16)
                    sp.dma_start(LB, t["ln1_b"].to_broadcast([P, D])).then_inc(ln1_ld, 16)
                    sp.dma_start(QB[:], q_d[0:1, :].to_broadcast([P, AW])).then_inc(qb_ld, 16)
                    sp.wait_ge(g_st, 16 * NB)
                    sp.wait_ge(small_ld, 16 * 9)
                    sp.wait_ge(cons_hi, 2)
                    sp.dma_start(GB[:].rearrange("p t h -> p (t h)"), G_d[0]).then_inc(gb_ld, 16)
                for n in (2 * c, 2 * c + 1):
                    if n >= 2:
                        pages(n, KR, n % 2, t["cache_k"], k_ld, k_red, n - 1)
                    else:
                        pages(n, KR, n % 2, t["cache_k"], k_ld)
            sp.wait_ge(k_mul, NCH)
            sp.dma_start(QB[:], q_d[1:2, :].to_broadcast([P, AW])).then_inc(qb_ld, 16)
            pages(0, VR, 0, t["cache_v"], v_ld)
            pages(1, VR, 1, t["cache_v"], v_ld)
            sp.wait_ge(wo_lo, OC)
            for s in range(WS):
                sp.dma_start(WR[:, s, :], t["ffn"][0, s]).then_inc(ffn_ld[s], 16)
            sp.wait_ge(m_max, 1)
            sp.dma_start(GB[:].rearrange("p t h -> p (t h)"), G_d[1]).then_inc(gb_ld, 16)
            sp.wait_ge(n1_b, RT)
            sp.wait_ge(vs_zero, 1)
            sp.dma_start(VS[0:NB, :], t["v_s"]).then_inc(vs_ld, 16)
            for s in range(2):
                sp.wait_ge(ffn_lo[s], 1)
                sp.dma_start(WR[:, s, :], t["ffn"][1, s]).then_inc(ffn_ld[s], 16)

            def iteration(i, last):
                for k in range(9):
                    r, s = k // 3, k % 3
                    f = i * 3 + (1 + r)
                    nxt = f if s == 2 else f + 1
                    if not (last and r == 2 and s < 2):
                        sp.wait_ge(ffn_lo[s], nxt)
                        sp.dma_start(WR[:, s, :], t["ffn"][bass.ds(nxt, 1), s].rearrange("a p n -> (a p) n")
                                     ).then_inc(ffn_ld[s], 16)
                    if k < NCH:
                        n = i * NCH + (NCH + k)
                        pages(n, KR, k % 2, t["cache_k"], k_ld, k_red, n - 1)
                    for c in VALUES_AFTER.get(k, ()):
                        pages(i * NCH + (c + 2), VR, c % 2, t["cache_v"], v_ld, v_used, i * NCH + (c + 1))
                if not last:
                    sp.wait_ge(m_max, i + 2)
                    sp.dma_start(GB[:].rearrange("p t h -> p (t h)"),
                                 G_d[bass.ds(i + 2, 1)].rearrange("a p n -> (a p) n")).then_inc(gb_ld, 16)
                    sp.wait_ge(k_mul, i * NCH + 2 * NCH)
                    sp.dma_start(QB[:], q_d[bass.ds(i + 2, 1), :].to_broadcast([P, AW])).then_inc(qb_ld, 16)

            with sp.Fori(0, NITER - 1) as i:
                iteration(i, False)
            iteration(NITER - 1, True)
            for c in range(NCH - 2):
                pages(NITER * NCH + c + 2, VR, c % 2, t["cache_v"], v_ld, v_used, NITER * NCH + c + 1)

            for s in range(WS):
                sp.wait_ge(ffn_lo[s], FT)
            sp.dma_start(LG2, t["ln2_g"].to_broadcast([P, D])).then_inc(ln2_ld, 16)
            sp.dma_start(LB2, t["ln2_b"].to_broadcast([P, D])).then_inc(ln2_ld, 16)
            sp.wait_ge(v_used, NB * NCH)
            for k in range(KC):
                if k >= 6:
                    sp.wait_ge(t_used, k - 5)
                sp.dma_start(TR[k % 6], t["w_o"][k * P:(k + 1) * P, :]).then_inc(t_ld[k % 6], 16)
                if k == 5:
                    sp.wait_ge(hl_done, FT)
                    sp.wait_ge(am_full, NB)
                    for dst, src in ((xs1, t["xs"]), (sg, t["ln1_g"].to_broadcast([NB, D])),
                                     (sbeta, t["ln1_b"].to_broadcast([NB, D]))):
                        sp.dma_start(dst, src).then_inc(e_ld, 16)

            def tiles(i, first):
                for q, (r, s) in enumerate(((0, 0), (0, 1), (1, 0), (1, 1), (0, 2), (1, 2))):
                    used = (KC - 2 + q + 1 if q < 2 else q + 1) if first else i * 6 + (KC - 6 + q + 1)
                    sp.wait_ge(t_used, used)
                    sp.dma_start(TR[q], t["ffn"][bass.ds(i * 2 + r, 1), s].rearrange("a p n -> (a p) n")
                                 ).then_inc(t_ld[q], 16)

            tiles(0, True)
            with sp.Fori(1, FT // 2) as i:
                tiles(i, False)
            sp.wait_ge(e_x1, 1)
            for dst, src in ((sg, t["ln2_g"]), (sbeta, t["ln2_b"])):
                sp.dma_start(dst, src.to_broadcast([NB, D])).then_inc(e_vec_ld, 16)
            sp.wait_ge(e_y, 1)
            sp.dma_start(t["y_s"], xs2).then_inc(e_st, 16)
            sp.wait_ge(e_st, 16)
            sp.wait_ge(y_st, 16 * RT)
            sp.wait_ge(misc_st, 16 * 4)
            sp.wait_ge(sn_st, 16 * 4)
            sp.wait_ge(kn_st, 16 * PAIRS)
            sp.wait_ge(vn_st, 16 * PAIRS)

        @block.gpsimd
        def _(pool):
            link = Chain(pool, pool_chain)
            for tile, value in ((ones, 1.0), (PN, 0.0), (PND, 0.0), (PD, 1.0)):
                pool.memset(tile[:], value).then_inc(consts, 1)
            pool.dma_start(page_row[:], t["page_row"]).then_inc(idx_ld, 16)
            pool.wait_ge(idx_ld, 16)
            for m in range(2):
                pool.indirect_dma_start(LF[:, m, :], None, t["logf"],
                                        bass.IndirectOffsetOnAxis(ap=page_row[:, m:m + 1].bitcast(U32), axis=0)
                                        ).then_inc(logf_ld, 16)
            pool.dma_start(t["p_s"][:, 0:STATE - 1, :], t["state3"][:, 1:STATE, :]).then_inc(misc_st, 16)
            pool.wait_ge(f_done, 2)
            pool.dma_start(negF_d, fnf[:, 0:ROWS]).then_inc(negF_st, 16)
            pool.wait_ge(ob_free, O["ft"] + 1)
            pool.dma_start(t["f_p"].rearrange("(i p) h -> p i h", p=P), f_rows[:, 0:RT, :]).then_inc(misc_st, 16)
            pool.dma_start(t["f_s"], f_rows[0:NB, RT, :]).then_inc(misc_st, 16)
            pool.wait_ge(tb_free, T[("g", 1)] + 1)
            for b in range(NB):
                pool.dma_start(G_d[b], GT[:, b // 4, (b % 4) * NPAGE * H:(b % 4 + 1) * NPAGE * H]).then_inc(g_st, 16)
            for p in range(PAIRS):
                for kind, src, dst, stored in (("kn", KN, t["k_p"], kn_st), ("vn", VN, t["v_p"], vn_st)):
                    pool.wait_ge(tb_free, T[(kind, p)] + 1)
                    pool.dma_start(dst[:, p * P:(p + 1) * P].rearrange("(i q) n -> q i n", q=P),
                                   src.rearrange("q (i n) -> q i n", i=RT)).then_inc(stored, 16)
            pool.wait_ge(tb_free, T[("ct", PAIRS - 1)] + 1)
            for n in range(3):
                pool.memset(UB[n][:, 0:16], 0.0).then_inc(pads, 1)
            pool.wait_ge(pads, 3)
            for g in range(GROUPS):
                pool.wait_ge(pb_free, U[("u", g)] + 1)
                if g >= 1:
                    pool.wait_ge(d_done, g)
                src = 0
                for n in range(g + 1):
                    dst = 2 if src == 1 else 1
                    ins = pool.tensor_tensor(UB[dst][:, 16:UW], UB[src][:, 16:UW],
                                             UB[src][:, 16 - 2 ** n:UW - 2 ** n], ALU.add)
                    if n < g:
                        link(ins)
                    else:
                        ins.then_inc(u_win, 1)
                    src = dst
            pool.wait_ge(tb_free, T[("un", GROUPS - 1)] + 1)
            pool.dma_start(t["p_p"], UN).then_inc(misc_st, 16)
            pool.wait_ge(pb_free, U[("sn", 1)] + 1)
            qkv = SN[:, 0:3 * PAIRS * P].rearrange("b (p c n) -> b c p n", p=PAIRS, c=3)
            for c, dst in enumerate((q_d, t["k_s"], t["v_s"])):
                pool.dma_start(dst.rearrange("b (p n) -> b p n", p=PAIRS), qkv[:, c]).then_inc(sn_st, 16)
            pool.dma_start(t["p_s"][:, STATE - 1, :], SN[:, 3 * PAIRS * P:]).then_inc(sn_st, 16)

            def multiply(c, loaded, q_loaded):
                pool.wait_ge(k_ld[c % 2], loaded)
                if c == 0:
                    pool.wait_ge(qb_ld, q_loaded)
                keys = KR[c % 2].rearrange("p (j n) -> p j n", j=CH)
                pool.tensor_tensor(keys, keys, QB[:].rearrange("p (o n) -> p o n", o=1).to_broadcast([P, CH, AW]),
                                   ALU.mult).then_inc(k_mul, 1)

            def rest(s, n):
                pool.wait_ge(ffn_hi[s], n)
                pool.tensor_tensor(WL[:, s, :], WR[:, s, :], WH[:, s, :].bitcast(F32), ALU.subtract
                                   ).then_inc(ffn_lo[s], 1)

            for c in range(NCH):
                multiply(c, 64 * (c // 2 + 1), 16)
            for s in range(WS):
                rest(s, 1)
            for i in range(RT):
                pool.wait_ge(n1_g, i + 1)
                pool.tensor_tensor(ACC[:, i, :], ACC[:, i, :], LB, ALU.add).then_inc(n1_b, 1)
            pool.wait_ge(n1_b, RT)
            pool.memset(VS, 0.0).then_inc(vs_zero, 1)
            for s in range(2):
                rest(s, 2)

            def iteration(i, last):
                for k in range(9):
                    r, s = k // 3, k % 3
                    if k < NCH:
                        multiply(k, i * 256 + 64 * (4 + k // 2 + 1), i * 16 + 32)
                    if not (last and r == 2 and s < 2):
                        rest(s, i * 3 + (2 + r if s == 2 else 3 + r))

            with pool.Fori(0, NITER - 1) as i:
                iteration(i, False)
            iteration(NITER - 1, True)

            for i in range(RT):
                pool.wait_ge(n2_g, i + 1)
                if i == 0:
                    pool.wait_ge(ln2_ld, 32)
                pool.tensor_tensor(ACC[:, i, :], ACC[:, i, :], LB2, ALU.add).then_inc(n2_b, 1)
                pool.wait_ge(n2_b, i + 1)
                pool.dma_start(t["y_p"][i * P:(i + 1) * P, :], ACC[:, i, :]).then_inc(y_st, 16)

        @block.scalar
        def _(act):
            def entry_hi(e):
                act.wait_ge(raw_ld[e % WS], 16 * (e // WS + 1))
                j = e - KC
                if j >= WS:
                    act.wait_ge(pb_full, tile_use[j - WS] + 1)
                act.copy(XH[:, e, :] if j < 0 else WH[:, j % WS, :], WR[:, e % WS, :]).then_inc(ent_hi, 1)

            act.wait_ge(xswf_ld, 32)
            act.copy(xsH[:].rearrange("p k n -> p (k n)"), xs_raw).then_inc(small_hi, 1)
            act.copy(wfH[:].rearrange("p k n -> p (k n)"), wf_raw).then_inc(small_hi, 1)
            for e in range(KC + WS):
                entry_hi(e)
            act.wait_ge(small_ld, 16 * 9)
            act.copy(identR[:], ident[:]).then_inc(cons_hi, 1)
            act.copy(causalR[:], causal).then_inc(cons_hi, 1)
            act.wait_ge(f_z, 1)
            act.activation(fb, fa, ACT.Exp, scale=-1.0).then_inc(f_t, 1)
            act.wait_ge(f_u, 1)
            act.activation(fa, fnf, ACT.Ln).then_inc(f_l, 1)

            for p in range(PAIRS):
                uq, uk = U[("q", p)], U[("k", p)]
                ps = pb(uq)
                act.wait_ge(pb_full, uq + 1)
                for hh in range(2):
                    a = slice(64 * hh, 64 * hh + 64)
                    act.copy(R2[a, 3 * hh, :], ps[a, :]).then_inc(q_hi, 1)
                ps = pb(uk)
                act.wait_ge(pb_full, uk + 1)
                if p >= 1:
                    act.wait_ge(tb_free, T[("ct", p - 1)] + 1)
                act.copy(KST, ps).then_inc(kst_done, 1)
                for hh in range(2):
                    a = slice(64 * hh, 64 * hh + 64)
                    b = slice(64 - 64 * hh, 128 - 64 * hh)
                    act.copy(R2[a, 3 * hh + 1, :], ps[a, :]).then_inc(k_hi, 1)
                    act.copy(R2[b, 3 * hh + 1, :], ps[a, :]).then_inc(k_hi, 1)
                entry_hi(KC + WS + 3 * p)
                act.wait_ge(tb_full, T[("kn", p)] + 1)
                if p >= 1:
                    act.wait_ge(kn_st, 16 * p)
                act.copy(KN, TB).then_inc(tb_free, 1)
                entry_hi(KC + WS + 3 * p + 1)
                entry_hi(KC + WS + 3 * p + 2)
                for s in range(STEPS + 2):
                    if s < STEPS:
                        w = (s % RT + 1) * P
                        act.wait_ge(pb_free, U[("s", p, s)] + 1)
                        act.activation(L[s % 2][:, 0:w], L[s % 2][:, 0:w], ACT.Exp, scale=-1.0,
                                       bias=negm[:, s % 2:s % 2 + 1], accum_out=rsum[:, s % 2:s % 2 + 1]
                                       ).then_inc(e_done, 1)
                    v = s - 1
                    if 0 <= v < STEPS and v % 2:
                        w = (v % RT + 1) * P
                        act.wait_ge(tb_full, T[("t", p, v)] + 1)
                        if STEPS * p + v >= 2:
                            act.wait_ge(ob_full, O[("pv", p, v - 2)] + 1 if v >= 2 else O[("pv", p - 1, STEPS + v - 2)] + 1)
                        act.copy(PT[1][:, 0:w], TB[:, 0:w]).then_inc(tb_free, 1)
                act.wait_ge(tb_full, T[("ct", p)] + 1)
                act.copy(ACC[:, p, :], TB).then_inc(tb_free, 1)
            entry_hi(KC + NWT - 1)

            for k in range(KC):
                if k == 0:
                    act.wait_ge(pb_full, U[("u", GROUPS - 1)] + 1)
                    act.wait_ge(tb_free, T[("ct", PAIRS - 1)] + 1)
                if k >= 4:
                    act.wait_ge(pb_free, U[("w", k - 4)] + 1)
                act.copy(XH[:, k, :], ACC[:, k, :]).then_inc(cat_hi, 1)
            for c in range(OC):
                act.wait_ge(wo_ld, 16 * (c + 1))
                if c >= 2:
                    act.wait_ge(pb_full, U[("o", c - 2, RT - 1)] + 1)
                src = WR[:, 0:2, :]
                act.copy((R2 if c % 2 else WH)[:, 0:2, :], src).then_inc(wo_hi, 1)

            def tile_hi(s, n, used, count):
                act.wait_ge(ffn_ld[s], n * 16)
                act.wait_ge(used, count)
                act.copy(WH[:, s, :], WR[:, s, :]).then_inc(ffn_hi[s], 1)

            for s in range(WS):
                tile_hi(s, 1, pb_full, U[("o", 2, RT - 1)] + 1)
            for i in range(RT + 3):
                if i < RT:
                    act.wait_ge(n1_var, i + 1)
                    act.activation(sd[:, i, 0:1], sd[:, i, 1:2], ACT.Sqrt).then_inc(n1_sd, 1)
                if 1 <= i <= RT:
                    v = i - 1
                    act.wait_ge(n1_rs, v + 1)
                    act.activation(ACC[:, v, :], ACC[:, v, :], ACT.Identity, scale=rs[:, v, 0:1],
                                   bias=rs[:, v, 1:2]).then_inc(n1_y, 1)
                if i >= 3:
                    v = i - 3
                    act.wait_ge(tb_full, T[("x1", v)] + 1)
                    act.copy(XH[:, :, v * P:(v + 1) * P], TB.rearrange("p (k n) -> p k n", k=KC)).then_inc(x1_hi, 1)
                    act.mul(ACC[:, v, :], ACC[:, v, :], ALPHA).then_inc(n1_alpha, 1)

            def silu(f):
                act.wait_ge(g_full, f + 1)
                act.wait_ge(hl_done, f)
                act.activation(GU, PSM[:, 0:2, :].rearrange("p a n -> p (a n)"), ACT.Silu).then_inc(silu_done, 1)

            def hidden_hi(f, buf):
                act.wait_ge(gu_done, f + 1)
                act.copy(R2[:, 2 * buf, :], GU).then_inc(hh_done, 1)

            def exponentials(b):
                act.wait_ge(m_sub, b * 2 + 2)
                act.activation(PR[:], PR[:], ACT.Exp).then_inc(m_exp, 1)
                act.activation(PN[0:NB, :], lsub[:], ACT.Exp).then_inc(m_exp, 1)

            silu(0)
            tile_hi(0, 2, g_full, 1)
            hidden_hi(0, 0)
            tile_hi(1, 2, u_full, 1)

            def iteration(i, last):
                for r in range(3):
                    f = i * 3 + (1 + r)
                    silu(f)
                    if not (last and r == 2):
                        tile_hi(0, f + 2, g_full, f + 1)
                    if r == 0:
                        exponentials(i)
                    hidden_hi(f, (1 + r) % 3)
                    if not (last and r == 2):
                        tile_hi(1, f + 2, u_full, f + 1)
                    tile_hi(2, f + 1, d_full, f * 16)

            with act.Fori(0, NITER - 1) as i:
                iteration(i, False)
            iteration(NITER - 1, True)
            exponentials(NITER)

            for i in range(RT + 1):
                if i < RT:
                    act.wait_ge(n2_var, i + 1)
                    act.activation(sd[:, i, 0:1], sd[:, i, 1:2], ACT.Sqrt).then_inc(n2_sd, 1)
                if i >= 1:
                    v = i - 1
                    act.wait_ge(n2_rs, v + 1)
                    act.activation(ACC[:, v, :], ACC[:, v, :], ACT.Identity, scale=rs[:, v, 0:1],
                                   bias=rs[:, v, 1:2]).then_inc(n2_y, 1)
            act.wait_ge(e_var, 1)
            act.activation(sd[0:NB, RT, 0:1], sd[0:NB, RT, 1:2], ACT.Sqrt).then_inc(e_sd, 1)

            def sample_silu(i):
                for r in range(2):
                    act.wait_ge(t_used, i * 6 + (KC + 2 * r + 2))
                    act.activation(hsilu[:, r, :], PSM[:, 4 + r, 0:NB], ACT.Silu).then_inc(e_silu, 1)

            with act.Fori(0, FT // 2) as i:
                sample_silu(i)
            act.wait_ge(e_var, 2)
            act.activation(sd[0:NB, RT, 0:1], sd[0:NB, RT, 1:2], ACT.Sqrt).then_inc(e_sd, 1)

        @block.tensor
        def _(pe):
            def claim(u):
                if u >= 2:
                    pe.wait_ge(pb_free, u - 1)
                return pb(u)

            def claim_tb(n):
                if n >= 1:
                    pe.wait_ge(tb_free, n)
                return TB

            def claim_ob(n):
                if n >= 1:
                    pe.wait_ge(ob_free, n)
                return OB

            PARTS = ((0, 0), (0, 1), (1, 0))

            def project(j, u):
                ps, w, x, xs = claim(u), (WH, WL), (XH, XL), (xsH, xsL)
                pe.wait_ge(ent_lo, KC + j + 1)
                for k in range(KC):
                    cols = slice(k * P, (k + 1) * P)
                    for n, (a, b) in enumerate(PARTS):
                        for half in range(2):
                            hc = slice(half * HALF, (half + 1) * HALF)
                            pe.matmul(ps[:, hc], w[a][:, j % WS, cols], x[b][:, k, hc],
                                      start=(k == 0 and n == 0), stop=(k == KC - 1 and n == 2))
                for k in range(KC):
                    for n, (a, b) in enumerate(PARTS):
                        ins = pe.matmul(B7[:, j * NB:(j + 1) * NB], w[a][:, j % WS, k * P:(k + 1) * P], xs[b][:, k, :],
                                        start=(k == 0 and n == 0), stop=(k == KC - 1 and n == 2))
                ins.then_inc(pb_full, 1)

            def turn(src, n=RT):
                for i in range(n):
                    ins = pe.transpose(TB[:, i * P:(i + 1) * P], src(i), ident[:])
                return ins

            w, x, xs = (wfH, wfL), (XH, XL), (xsH, xsL)
            pe.wait_ge(small_lo, 2)
            for k in range(KC):
                pe.wait_ge(ent_lo, k + 1)
                for n, (a, b) in enumerate(PARTS):
                    for half in range(2):
                        hc = slice(half * HALF, (half + 1) * HALF)
                        ins = pe.matmul(pb(0)[0:H, hc], w[a][:, k, :], x[b][:, k, hc],
                                        start=(k == 0 and n == 0), stop=(k == KC - 1 and n == 2))
            ins.then_inc(pb_full, 1)
            for k in range(KC):
                for n, (a, b) in enumerate(PARTS):
                    ins = pe.matmul(OB[0:H, 0:NB], w[a][:, k, :], xs[b][:, k, :],
                                    start=(k == 0 and n == 0), stop=(k == KC - 1 and n == 2))
            ins.then_inc(ob_full, 1)

            for p in range(PAIRS):
                project(3 * p, U[("q", p)])
                if p == 0:
                    pe.wait_ge(small_ld, 16 * 9)
                    pe.wait_ge(f_done, 1)
                    ob = claim_ob(O["ft"])
                    for i in range(RT):
                        pe.transpose(ob[:, i * H:(i + 1) * H], fz[:, i * P:(i + 1) * P], ident[0:H, 0:H])
                    pe.transpose(ob[0:NB, RT * H:(RT + 1) * H], fz[:, ROWS:FRW], ident[0:H, 0:H]).then_inc(ob_full, 1)
                project(3 * p + 1, U[("k", p)])
                if p == 0:
                    pe.wait_ge(suf_scan, 2)
                    ob = claim_ob(O["c"])
                    for m in range(2):
                        ins = pe.matmul(ob[:, m * H:(m + 1) * H], cum, suftot[:, m, :], start=True, stop=True)
                    ins.then_inc(ob_full, 1)
                project(3 * p + 2, U[("v", p)])
                if p == 0:
                    for m in range(2):
                        pe.wait_ge(ob_free, O["c"] + 1)
                        claim_tb(T[("g", m)])
                        turn(lambda h: LS[:, m, h * P:(h + 1) * P]).then_inc(tb_full, 1)
                claim_tb(T[("kn", p)])
                pe.wait_ge(kst_done, p + 1)
                turn(lambda i: KST[:, i * P:(i + 1) * P]).then_inc(tb_full, 1)
                claim_tb(T[("vn", p)])
                pe.wait_ge(pb_free, U[("v", p)] + 1)
                turn(lambda i: VST[:, i * P:(i + 1) * P]).then_inc(tb_full, 1)
                pe.wait_ge(pb_free, U[("k", p)] + 1)
                pe.wait_ge(cons_hi, 2)
                for s in range(STEPS + 2):
                    if s < STEPS:
                        hh, i = s // RT, s % RT
                        ps, w = claim(U[("s", p, s)]), (i + 1) * P
                        for c in range(0, w, HALF):
                            n = min(HALF, w - c)
                            diag = c + n == w
                            for part in (1, 2):
                                ins = pe.matmul(ps[:, c:c + n], R2[:, 3 * hh, i * P:(i + 1) * P],
                                                R2[:, 3 * hh + part, c:c + n], start=(part == 1),
                                                stop=(part == 2 and not diag))
                            if diag:
                                ins = pe.matmul(ps[:, w - P:w], identR[:], causalR[:], start=False, stop=True)
                        ins.then_inc(pb_full, 1)
                    v = s - 1
                    if 0 <= v < STEPS:
                        claim_tb(T[("t", p, v)])
                        pe.wait_ge(e_done, STEPS * p + v + 1)
                        turn(lambda i: L[v % 2][:, i * P:(i + 1) * P], n=v % RT + 1).then_inc(tb_full, 1)
                    v = s - 2
                    if v >= 0:
                        hh, i = v // RT, v % RT
                        ob = claim_ob(O[("pv", p, v)])
                        pe.wait_ge(tb_free, T[("t", p, v)] + 1)
                        for kt in range(i + 1):
                            ins = pe.matmul(ob[:, 0:HD], PT[v % 2][:, kt * P:(kt + 1) * P],
                                            VN[:, kt * P + hh * HD:kt * P + hh * HD + HD],
                                            start=(kt == 0), stop=(kt == i))
                        ins.then_inc(ob_full, 1)
                claim_tb(T[("ct", p)])
                pe.wait_ge(ob_free, O[("pv", p, STEPS - 1)] + 1)
                turn(lambda i: KST[:, i * P:(i + 1) * P]).then_inc(tb_full, 1)

            def mixer(g):
                pe.wait_ge(d_done, g + 1)
                ps = claim(U[("w", g)])
                if g == 0:
                    pe.wait_ge(mix_ld, 16 * 4)
                for half in range(2):
                    hc = slice(half * HALF, (half + 1) * HALF)
                    ins = pe.matmul(ps[:, hc], WP[:, g, :], DB[:, hc], start=True, stop=True)
                ins.then_inc(pb_full, 1)
                claim_tb(T[("un", g)])
                pe.transpose(TB[0:STATE, 0:P], UB[0][:, UW - STATE:UW], ident[:]).then_inc(tb_full, 1)

            for g in range(GROUPS):
                project(3 * PAIRS + g, U[("u", g)])
                if g >= 1:
                    mixer(g - 1)
            mixer(GROUPS - 1)
            pe.wait_ge(sst_done, 1)
            for m in range(2):
                ps = claim(U[("sn", m)])
                for j in range(8):
                    ins = pe.transpose(ps[0:NB, j * P:(j + 1) * P], SST[:, 8 * m + j, :], ident[:])
                ins.then_inc(pb_full, 1)
            ob = claim_ob(O["sp"])
            for g in range(GROUPS):
                ins = pe.matmul(ob[:, g * NB:(g + 1) * NB], STT[:, g * P:(g + 1) * P], SEL[:, g, :], start=True, stop=True)
            ins.then_inc(ob_full, 1)
            ob = claim_ob(O["sw"])
            pe.wait_ge(sd_done, 1)
            for g in range(GROUPS):
                ins = pe.matmul(ob[:, g * NB:(g + 1) * NB], WP[:, g, :], SD[:, g, :], start=True, stop=True)
            ins.then_inc(ob_full, 1)

            for c in range(OC):
                hi, lo = (R2[:, 0:2, :], R2[:, 2:4, :]) if c % 2 else (WH[:, 0:2, :], WL[:, 0:2, :])
                wo = [part.rearrange("p a (b n) -> p (a b) n", n=OCW) for part in (hi, lo)]
                pe.wait_ge(wo_lo, c + 1)
                for i in range(RT + (3 if c == OC - 1 else 0)):
                    if i < RT:
                        ps = claim(U[("o", c, i)])
                        for k in range(KC):
                            if c == 0 and i == 0:
                                pe.wait_ge(cat_lo, k + 1)
                            for n, (a, b) in enumerate(PARTS):
                                ins = pe.matmul(ps[:, 0:OCW], (XH, XL)[a][:, k, i * P:(i + 1) * P], wo[b][:, k, :],
                                                start=(k == 0 and n == 0), stop=(k == KC - 1 and n == 2))
                        ins.then_inc(pb_full, 1)
                    if c == OC - 1 and i >= 3:
                        v = i - 3
                        claim_tb(T[("x1", v)])
                        pe.wait_ge(n1_b, v + 1)
                        turn(lambda k: ACC[:, v, k * P:(k + 1) * P]).then_inc(tb_full, 1)

            def product(s, bank, f, done):
                pe.wait_ge(ffn_lo[s], f + 1)
                out = PSM[:, bank:bank + 2, :].rearrange("p a n -> p (a n)")
                for k in range(KC):
                    for n, (a, b) in enumerate(PARTS):
                        for half in range(2):
                            hc = slice(half * HALF, (half + 1) * HALF)
                            ins = pe.matmul(out[:, hc], (WH, WL)[a][:, s, k * P:(k + 1) * P], (XH, XL)[b][:, k, hc],
                                            start=(k == 0 and n == 0), stop=(k == KC - 1 and n == 2))
                ins.then_inc(done, 1)

            def down(f, buf):
                pe.wait_ge(ffn_lo[2], f + 1)
                pe.wait_ge(hl_done, f + 1)
                for n in range(2 * RT):
                    i, half = n // 2, n % 2
                    pe.wait_ge(d_free, f * 16 + (n + 1))
                    for m, (a, b) in enumerate(PARTS):
                        ins = pe.matmul(PSM[:, 4 + n % 2, :], R2[:, 2 * buf + a, i * P:(i + 1) * P],
                                        (WH, WL)[b][:, 2, half * HALF:(half + 1) * HALF],
                                        start=(m == 0), stop=(m == 2))
                    ins.then_inc(d_full, 1)

            def maximum(b):
                pe.wait_ge(m_max, b + 1)
                pe.transpose(PSM[0:H, 6, 0:P], mxp[:], ident[:]).then_inc(m_t, 1)

            def spread_maximum(b):
                pe.wait_ge(m_dg, b + 1)
                pe.matmul(PSM[:, 7, 0:H], ones[0:H, :], dg[:], start=True, stop=True).then_inc(m_b, 1)

            def denominator(b):
                pe.wait_ge(m_sum, b * 2 + 2)
                pe.matmul(PSM[:, 7, 16:17], PD[:].rearrange("p a n -> p (a n)"), ones[:, 0:1], start=True, stop=False)
                pe.matmul(PSM[:, 7, 16:17], PND[:].rearrange("p a n -> p (a n)"), ones[:, 0:1],
                          start=False, stop=True).then_inc(den_full, 1)

            def values(c, loaded):
                pe.wait_ge(v_ld[c % 2], loaded)
                last = c == NCH - 1
                if last:
                    pe.matmul(PSM[0:H, 6, :], PN[:], VS, start=False, stop=False, skip_group_check=True)
                for j in range(CH):
                    ins = pe.matmul(PSM[32 * j:32 * j + H, 6, :], PR[:, c * CH + j, :], VR[c % 2][:, j * AW:(j + 1) * AW],
                                    start=(c == 0), stop=last, skip_group_check=True)
                ins.then_inc(v_used, 1)

            def to_columns(b):
                pe.wait_ge(am_done, b + 1)
                pe.wait_ge(den_inv, b + 1)
                for c in range(AW // P):
                    ins = pe.matmul(PSM[:, 7, 32 + c:33 + c], AM[:, c * P:(c + 1) * P], ones[:, 0:1], start=True, stop=True)
                ins.then_inc(am_full, 1)

            pe.wait_ge(consts, 4)
            claim_ob(O["sw"] + 1)
            for n in range(AW // P):
                ins = pe.matmul(PSM[:, 6, n * P:(n + 1) * P], PND[:].rearrange("p a n -> p (a n)"), ident[:], start=True, stop=True)
            ins.then_inc(bank6_zero, 1)
            maximum(0)
            pe.wait_ge(pb_free, len(U))
            pe.wait_ge(tb_free, len(T))
            product(0, 0, 0, g_full)
            product(1, 2, 0, u_full)

            def iteration(i, last):
                for k in range(9):
                    r, s = k // 3, k % 3
                    f = i * 3 + (1 + r)
                    if s == 0:
                        pe.wait_ge(silu_done, f)
                        product(0, 0, f, g_full)
                    elif s == 1:
                        pe.wait_ge(gu_done, f)
                        product(1, 2, f, u_full)
                    else:
                        down(f - 1, r)
                    if k == 0:
                        spread_maximum(i)
                    if k == 1:
                        denominator(i)
                        pe.wait_ge(vs_ld, 16)
                    for c in VALUES_AFTER.get(k, ()):
                        values(c, i * 256 + 64 * (c // 2 + 1))
                to_columns(i)
                maximum(i + 1)

            with pe.Fori(0, NITER - 1) as i:
                iteration(i, False)
            iteration(NITER - 1, True)
            spread_maximum(NITER)
            down(FT - 1, 0)
            denominator(NITER)
            for c in range(NCH):
                values(c, NITER * 256 + 64 * (c // 2 + 1))
            to_columns(NITER)

            pe.wait_ge(am_cs, NB)
            pe.wait_ge(gu_done, FT)
            mix = PSM[0:NB, 0:2, :].rearrange("p a n -> p (a n)")
            for k in range(KC):
                pe.wait_ge(t_ld[k % 6], 16 * (k // 6 + 1))
                for half in range(2):
                    hc = slice(half * HALF, (half + 1) * HALF)
                    ins = pe.matmul(mix[:, hc], CS[:, k, :], TR[k % 6][:, hc], start=(k == 0), stop=(k == KC - 1))
                ins.then_inc(t_used, 1)
            pe.wait_ge(e_x1, 1)
            for k in range(KC):
                ins = pe.transpose(PSM[:, 2, k * NB:(k + 1) * NB], xs1[:, k * P:(k + 1) * P], ident[0:NB, 0:NB])
            ins.then_inc(e_t, 1)
            pe.wait_ge(e_xt, 1)
            pe.wait_ge(d_free, FT * 16 + 2)

            def sample_tiles(i, first, last):
                for q in range(4):
                    r, s = q // 2, q % 2
                    pe.wait_ge(t_ld[q], i * 16 + (48 if q < 2 else 32))
                    if not first and s == 0:
                        pe.wait_ge(e_hid, i * 2 + (r - 1))
                    for k in range(KC):
                        ins = pe.matmul(PSM[:, 4 + r, s * NB:(s + 1) * NB], TR[q][:, k * P:(k + 1) * P], CS[:, k, :],
                                        start=(k == 0), stop=(k == KC - 1))
                    ins.then_inc(t_used, 1)
                for r in range(2):
                    pe.wait_ge(t_ld[4 + r], i * 16 + 32)
                    pe.wait_ge(e_hid, i * 2 + (r + 1))
                    for half in range(2):
                        hc = slice(half * HALF, (half + 1) * HALF)
                        ins = pe.matmul(mix[:, hc], hid[:, r, :], TR[4 + r][:, hc], start=(first and r == 0),
                                        stop=(last and r == 1))
                    ins.then_inc(t_used, 1)

            sample_tiles(0, True, False)
            with pe.Fori(1, FT // 2 - 1) as i:
                sample_tiles(i, False, False)
            sample_tiles(FT // 2 - 1, False, True)

        @block.vector
        def _(dve):
            link = Chain(dve, dve_chain)

            def entry_lo(e):
                dve.wait_ge(ent_hi, e + 1)
                j = e - KC
                hi = XH[:, e, :] if j < 0 else WH[:, j % WS, :]
                dve.tensor_tensor(XL[:, e, :] if j < 0 else WL[:, j % WS, :], WR[:, e % WS, :], hi.bitcast(F32),
                                  ALU.subtract).then_inc(ent_lo, 1)

            dve.wait_ge(small_hi, 2)
            dve.tensor_tensor(xsL[:].rearrange("p k n -> p (k n)"), xs_raw,
                              xsH[:].rearrange("p k n -> p (k n)").bitcast(F32), ALU.subtract).then_inc(small_lo, 1)
            dve.tensor_tensor(wfL[:].rearrange("p k n -> p (k n)"), wf_raw,
                              wfH[:].rearrange("p k n -> p (k n)").bitcast(F32), ALU.subtract).then_inc(small_lo, 1)
            for e in range(KC + WS):
                entry_lo(e)
            dve.wait_ge(small_ld, 16 * 9)
            link(dve.memset(fone, 1.0))
            dve.wait_ge(pb_full, 1)
            dve.tensor_scalar(fz[:, 0:ROWS], pb(0)[0:H, :], bfc[:], None, ALU.add).then_inc(pb_free, 1)
            dve.wait_ge(ob_full, O["fs"] + 1)
            dve.tensor_scalar(fz[:, ROWS:FRW], OB[0:H, 0:NB], bfc[:], None, ALU.add).then_inc(ob_free, 1)
            dve.wait_ge(pb_free, 1)
            dve.wait_ge(ob_free, 1)
            dve.scalar_tensor_tensor(out=fa, in0=fz, scalar=-1.0, in1=fz, op0=ALU.mult, op1=ALU.max).then_inc(f_z, 1)
            dve.wait_ge(f_t, 1)
            dve.tensor_scalar(fnf, fb, 1.0, None, ALU.add).then_inc(f_u, 1)
            dve.wait_ge(f_l, 1)
            link(dve.tensor_scalar(fnf, fnf, -1.0, None, ALU.add))
            link(dve.tensor_tensor(fnf, fb, fnf, ALU.subtract))
            link(dve.tensor_tensor(fa, fa, fnf, ALU.add))
            link(dve.tensor_single_scalar(fz, fz, 0.0, ALU.min))
            dve.tensor_tensor(fz, fz, fa, ALU.subtract).then_inc(f_done, 1)
            dve.wait_ge(f_done, 1)
            link(dve.tensor_tensor_scan(fnf[:, 0:ROWS], fone, fz[:, 0:ROWS], 0.0, ALU.mult, ALU.subtract))
            dve.tensor_scalar(fnf[:, 0:ROWS], fnf[:, 0:ROWS], 1.0 / SCALE, None, ALU.mult).then_inc(f_done, 1)
            dve.wait_ge(logf_ld, 32)
            for m in range(2):
                link(dve.tensor_tensor_scan(LS[:, m, :], scanmask, LF[:, m, :], 0.0, ALU.mult, ALU.add))
                dve.tensor_copy(suftot[:, m, :], LS[:, m, :].rearrange("p (h k) -> p h k", h=H)[:, :, P - 1]
                                ).then_inc(suf_scan, 1)

            for p in range(PAIRS):
                ps = pb(U[("q", p)])
                for hh in range(2):
                    a, b = slice(64 * hh, 64 * hh + 64), slice(64 - 64 * hh, 128 - 64 * hh)
                    dve.wait_ge(q_hi, 2 * p + hh + 1)
                    ins = dve.tensor_tensor(R2[b, 3 * hh, :], ps[a, :], R2[a, 3 * hh, :].bitcast(F32), ALU.subtract)
                ins.then_inc(pb_free, 1)
                if p == 0:
                    dve.wait_ge(ob_full, O["ft"] + 1)
                    link(dve.tensor_copy(f_rows[:, 0:RT, :].rearrange("p i h -> p (i h)"), OB[:, 0:RT * H]))
                    dve.tensor_copy(f_rows[0:NB, RT, :], OB[0:NB, RT * H:(RT + 1) * H]).then_inc(ob_free, 1)
                ps = pb(U[("k", p)])
                for hh in range(2):
                    a, b = slice(64 * hh, 64 * hh + 64), slice(64 - 64 * hh, 128 - 64 * hh)
                    dve.wait_ge(k_hi, 4 * p + 2 * hh + 2)
                    for dst in (a, b):
                        ins = dve.tensor_tensor(R2[dst, 3 * hh + 2, :], ps[a, :], R2[a, 3 * hh + 1, :].bitcast(F32),
                                                ALU.subtract)
                ins.then_inc(pb_free, 1)
                if p == 0:
                    dve.wait_ge(ob_full, O["c"] + 1)
                    for m in range(2):
                        ls = LS[:, m, :].rearrange("p (h k) -> p h k", h=H)
                        tot = OB[:, m * H:(m + 1) * H].rearrange("p (h o) -> p h o", o=1).to_broadcast([P, H, P])
                        ins = dve.tensor_tensor(ls, tot, ls, ALU.subtract)
                    ins.then_inc(ob_free, 1)
                entry_lo(KC + WS + 3 * p)
                dve.wait_ge(pb_full, U[("v", p)] + 1)
                dve.tensor_copy(VST, pb(U[("v", p)])).then_inc(pb_free, 1)
                if p == 0:
                    for m in range(2):
                        dve.wait_ge(tb_full, T[("g", m)] + 1)
                        dve.tensor_copy(GT[:, m, :].rearrange("p (r h) -> p r h", h=H),
                                        TB.rearrange("p (h r) -> p r h", h=H)).then_inc(tb_free, 1)
                entry_lo(KC + WS + 3 * p + 1)
                dve.wait_ge(tb_full, T[("vn", p)] + 1)
                if p >= 1:
                    dve.wait_ge(vn_st, 16 * p)
                dve.tensor_copy(VN, TB).then_inc(tb_free, 1)
                entry_lo(KC + WS + 3 * p + 2)
                for s in range(STEPS + 2):
                    if s < STEPS:
                        hh, i = s // RT, s % RT
                        u, w = U[("s", p, s)], (i + 1) * P
                        dve.wait_ge(pb_full, u + 1)
                        if i == 0:
                            dve.wait_ge(nf_ld[hh], 16 * (p + 1))
                        if STEPS * p + s >= 2:
                            dve.wait_ge(tb_full, T[("t", p, s - 2) if s >= 2 else ("t", p - 1, STEPS + s - 2)] + 1)
                        dve.tensor_tensor_reduce(L[s % 2][:, 0:w], pb(u)[:, 0:w], NF[hh][:, 0:w], -SCALE, 3e38,
                                                 ALU.add, ALU.min, negm[:, s % 2:s % 2 + 1]).then_inc(pb_free, 1)
                    v = s - 1
                    if 0 <= v < STEPS:
                        if v % 2 == 0:
                            w = (v % RT + 1) * P
                            dve.wait_ge(tb_full, T[("t", p, v)] + 1)
                            if STEPS * p + v >= 2:
                                dve.wait_ge(ob_full, O[("pv", p, v - 2) if v >= 2 else ("pv", p - 1, STEPS + v - 2)] + 1)
                            dve.tensor_copy(PT[0][:, 0:w], TB[:, 0:w]).then_inc(tb_free, 1)
                        dve.wait_ge(e_done, STEPS * p + v + 1)
                        if STEPS * p + v >= 2:
                            dve.wait_ge(ob_free, O[("pv", p, v - 2) if v >= 2 else ("pv", p - 1, STEPS + v - 2)] + 1)
                        dve.reciprocal(rinv[:, v % 2:v % 2 + 1], rsum[:, v % 2:v % 2 + 1]).then_inc(inv_done, 1)
                    v = s - 2
                    if v >= 0:
                        hh, i = v // RT, v % RT
                        dve.wait_ge(ob_full, O[("pv", p, v)] + 1)
                        dve.wait_ge(inv_done, STEPS * p + v + 1)
                        dve.tensor_scalar(KST[:, i * P + hh * HD:i * P + hh * HD + HD], OB[:, 0:HD],
                                          rinv[:, v % 2:v % 2 + 1], None, ALU.mult).then_inc(ob_free, 1)
            entry_lo(KC + NWT - 1)

            def finish_group(g):
                dve.wait_ge(pb_full, U[("w", g)] + 1)
                if g == 0:
                    dve.wait_ge(g_st, 16 * NB)
                dve.tensor_scalar(ACC[:, GROUPS + g, :], pb(U[("w", g)]), psc[:, g:g + 1], None, ALU.mult
                                  ).then_inc(pb_free, 1)
                dve.wait_ge(tb_full, T[("un", g)] + 1)
                dve.tensor_copy(UN[:, g * P:(g + 1) * P], TB[0:STATE, 0:P]).then_inc(tb_free, 1)

            for g in range(GROUPS):
                w = 2 ** (g + 1)
                dve.wait_ge(pb_full, U[("u", g)] + 1)
                if g == 0:
                    dve.wait_ge(pads, 3)
                else:
                    dve.wait_ge(tb_full, T[("un", g - 1)] + 1)
                dve.tensor_copy(UB[0][:, 16:UW], pb(U[("u", g)])).then_inc(pb_free, 1)
                if g == 0:
                    dve.wait_ge(mix_ld, 16 * 4)
                dve.wait_ge(u_win, g + 1)
                if g >= 1:
                    dve.wait_ge(pb_full, U[("w", g - 1)] + 1)
                win = UB[1 + g % 2]
                dve.wait_ge(pb_free, U[("u", g)] + 1)
                link(dve.tensor_tensor(DB[:, 0:16], win[:, 16:32], RC[:, g, :], ALU.mult))
                link(dve.tensor_tensor(DB[:, 0:16], DB[:, 0:16], UB[0][:, 16:32], ALU.subtract))
                dve.scalar_tensor_tensor(out=DB[:, 16:], in0=win[:, 32:UW], scalar=1.0 / w, in1=UB[0][:, 32:UW],
                                         op0=ALU.mult, op1=ALU.subtract).then_inc(d_done, 1)
                if g >= 1:
                    finish_group(g - 1)
            finish_group(GROUPS - 1)
            dve.wait_ge(pb_full, U[("u", GROUPS - 1)] + 1)
            dve.tensor_copy(SST.rearrange("p j b -> p (j b)"), B7[:, 0:NWT * NB]).then_inc(sst_done, 1)
            for m in range(2):
                dve.wait_ge(pb_full, U[("sn", m)] + 1)
                dve.tensor_copy(SN[:, m * D:(m + 1) * D], pb(U[("sn", m)])[0:NB, :]).then_inc(pb_free, 1)
            dve.wait_ge(sst_done, 1)
            dve.wait_ge(ob_full, O["sp"] + 1)
            us = SST[:, 3 * PAIRS:, :]
            dve.tensor_tensor(SS, OB[:, 0:GROUPS * NB].rearrange("p (g b) -> p g b", g=GROUPS), us, ALU.add
                              ).then_inc(ob_free, 1)
            dve.wait_ge(ob_free, O["sp"] + 1)
            for g in range(GROUPS):
                ins = dve.scalar_tensor_tensor(out=SD[:, g, :], in0=SS[:, g, :], scalar=0.5 ** (g + 1), in1=us[:, g, :],
                                               op0=ALU.mult, op1=ALU.subtract)
            ins.then_inc(sd_done, 1)
            dve.wait_ge(ob_full, O["sw"] + 1)
            for g in range(GROUPS):
                ins = dve.tensor_scalar(CS[:, GROUPS + g, :], OB[:, g * NB:(g + 1) * NB], psc[:, g:g + 1], None, ALU.mult)
            ins.then_inc(ob_free, 1)
            dve.wait_ge(pb_free, U[("sn", 1)] + 1)
            qkv = SN[:, 0:3 * PAIRS * P].rearrange("b (p c n) -> b c p n", p=PAIRS, c=3)
            link(dve.tensor_tensor(PROD.rearrange("b (p n) -> b p n", p=PAIRS), qkv[:, 0], qkv[:, 1], ALU.mult))
            link(dve.tensor_reduce(snew[:], PROD.rearrange("b (h n) -> b h n", h=H), AX.X, ALU.add))
            link(dve.scalar_tensor_tensor(out=snew[:], in0=snew[:], scalar=SCALE, in1=f_rows[0:NB, RT, :],
                                          op0=ALU.mult, op1=ALU.subtract))
            link(dve.tensor_tensor(LNEW[:], nmask, snew[:].rearrange("b (o h) -> b o h", o=1).to_broadcast([NB, NB, H]),
                                   ALU.add))

            for k in range(KC):
                dve.wait_ge(cat_hi, k + 1)
                dve.tensor_tensor(XL[:, k, :], ACC[:, k, :], XH[:, k, :].bitcast(F32), ALU.subtract).then_inc(cat_lo, 1)

            def output_lo(c):
                dve.wait_ge(wo_hi, c + 1)
                hi, lo = (R2[:, 0:2, :], R2[:, 2:4, :]) if c % 2 else (WH[:, 0:2, :], WL[:, 0:2, :])
                dve.tensor_tensor(lo, WR[:, 0:2, :], hi.bitcast(F32), ALU.subtract).then_inc(wo_lo, 1)

            def output(c, i):
                u = U[("o", c, i)]
                dve.wait_ge(pb_full, u + 1)
                cols = ACC[:, i, c * OCW:(c + 1) * OCW]
                dve.scalar_tensor_tensor(out=cols, in0=cols, scalar=ALPHA, in1=pb(u)[:, 0:OCW],
                                         op0=ALU.mult, op1=ALU.add).then_inc(pb_free, 1)

            def reduce_keys(c, multiplied):
                dve.wait_ge(k_mul, multiplied)
                dve.tensor_reduce(SC[:, c * CH:(c + 1) * CH, :].rearrange("p j h -> p (j h)"),
                                  KR[c % 2].rearrange("p (a n) -> p a n", n=HD), AX.X, ALU.add).then_inc(k_red, 1)

            def statistics(i, rows, src, done):
                for half in range(2):
                    ins = dve.bn_stats(st[0:rows, half, :], src[:, half * HALF:(half + 1) * HALF])
                link(ins)
                link(dve.bn_aggr(mv[0:rows, i, :], st[0:rows, :, :].rearrange("p a n -> p (a n)")))
                dve.tensor_scalar(sd[0:rows, i, 1:2], mv[0:rows, i, 1:2], EPS, None, ALU.add).then_inc(done, 1)

            def inverse(i, rows, done):
                link(dve.reciprocal(rs[0:rows, i, 0:1], sd[0:rows, i, 0:1]))
                dve.scalar_tensor_tensor(out=rs[0:rows, i, 1:2], in0=mv[0:rows, i, 0:1], scalar=-1.0,
                                         in1=rs[0:rows, i, 0:1], op0=ALU.mult, op1=ALU.mult).then_inc(done, 1)

            output_lo(0)
            output_lo(1)
            dve.wait_ge(x_ld, 16 * RT)
            for c in range(OC - 1):
                for i in range(RT):
                    output(c, i)
                    if i % 4 == 3:
                        n = 2 * c + i // 4
                        reduce_keys(n, n + 1)
                if c + 2 < OC:
                    output_lo(c + 2)
            for s in range(RT + 3):
                if s < RT:
                    output(OC - 1, s)
                    dve.wait_ge(pb_free, U[("o", OC - 1, s)] + 1)
                    statistics(s, P, ACC[:, s, :], n1_var)
                if 1 <= s <= RT:
                    v = s - 1
                    dve.wait_ge(n1_sd, v + 1)
                    inverse(v, P, n1_rs)
                if 2 <= s <= RT + 1:
                    v = s - 2
                    dve.wait_ge(n1_y, v + 1)
                    dve.wait_ge(ln1_ld, 32)
                    dve.tensor_tensor(ACC[:, v, :], ACC[:, v, :], LG, ALU.mult).then_inc(n1_g, 1)
                if s >= 3:
                    v = s - 3
                    cols = slice(v * P, (v + 1) * P)
                    dve.wait_ge(x1_hi, v + 1)
                    dve.tensor_tensor(XL[:, :, cols], TB.rearrange("p (k n) -> p k n", k=KC),
                                      XH[:, :, cols].bitcast(F32), ALU.subtract).then_inc(tb_free, 1)
                if s in (3, 7):
                    n = 6 + s // 4
                    reduce_keys(n, n + 1)

            def row_maximum(b):
                dve.wait_ge(k_red, b * NCH + NCH)
                dve.wait_ge(gb_ld, b * 16 + 16)
                link(dve.scalar_tensor_tensor(out=SC[:], in0=SC[:], scalar=SCALE, in1=GB[:], op0=ALU.mult, op1=ALU.add))
                link(dve.tensor_reduce(mxp[:], SC[:].rearrange("p t h -> p h t"), AX.X, ALU.max))
                dve.tensor_tensor(mxp[0:NB, :], mxp[0:NB, :], LNEW[:, bass.ds(b, 1), :].rearrange("p o h -> p (o h)"),
                                  ALU.max).then_inc(m_max, 1)

            def head_maximum(b):
                dve.wait_ge(m_t, b + 1)
                link(dve.tensor_reduce(gm[:], PSM[0:H, 6, 0:P], AX.X, ALU.max))
                dve.tensor_scalar(dg[:], ident[0:H, 0:H], gm[:], None, ALU.mult).then_inc(m_dg, 1)

            def subtract_maximum(b):
                dve.wait_ge(m_b, b + 1)
                link(dve.tensor_copy(Mb[:], PSM[:, 7, 0:H]))
                dve.tensor_tensor(PR[:], SC[:], Mb[:].rearrange("p (o h) -> p o h", o=1).to_broadcast([P, NPAGE, H]),
                                  ALU.subtract).then_inc(m_sub, 1)
                dve.tensor_tensor(lsub[:], LNEW[:, bass.ds(b, 1), :].rearrange("p o h -> p (o h)"), Mb[0:NB, :],
                                  ALU.subtract).then_inc(m_sub, 1)

            def sum_probabilities(b):
                dve.wait_ge(m_exp, b * 2 + 2)
                link(dve.tensor_reduce(psum_row[:], PR[:].rearrange("p t h -> p h t"), AX.X, ALU.add))
                for dst, src, rows in ((PD, psum_row, P), (PND, PN, NB)):
                    dve.tensor_copy(dst[0:rows, :, 0:H], src[0:rows, :].rearrange("p (o h) -> p o h", o=1
                                    ).to_broadcast([rows, 4, H])).then_inc(m_sum, 1)

            def invert_denominator(b):
                dve.wait_ge(den_full, b + 1)
                dve.reciprocal(rden[:], PSM[:, 7, 16:17]).then_inc(den_inv, 1)

            def own_heads(b):
                dve.wait_ge(v_used, b * NCH + NCH)
                dve.wait_ge(den_inv, b + 1)
                dve.scalar_tensor_tensor(out=AM.rearrange("p (h n) -> p h n", h=H),
                                         in0=PSM[:, 6, :].rearrange("p (h n) -> p h n", h=H), scalar=rden[:],
                                         in1=blkmask[:].rearrange("p (h o) -> p h o", o=1).to_broadcast([P, H, HD]),
                                         op0=ALU.mult, op1=ALU.mult).then_inc(am_done, 1)

            def keep_columns(b):
                dve.wait_ge(am_full, b + 1)
                dve.tensor_copy(CS[:, 0:AW // P, bass.ds(b, 1)].rearrange("p k o -> p (k o)"), PSM[:, 7, 32:32 + AW // P]
                                ).then_inc(am_cs, 1)

            def gate_times_up(f):
                dve.wait_ge(silu_done, f + 1)
                dve.wait_ge(u_full, f + 1)
                dve.tensor_tensor(GU, GU, PSM[:, 2:4, :].rearrange("p a n -> p (a n)"), ALU.mult).then_inc(gu_done, 1)

            def hidden_lo(f, buf):
                dve.wait_ge(hh_done, f + 1)
                dve.tensor_tensor(R2[:, 2 * buf + 1, :], GU, R2[:, 2 * buf, :].bitcast(F32), ALU.subtract
                                  ).then_inc(hl_done, 1)

            def add_down(f):
                dve.wait_ge(d_free, f * 16 + 2)
                for n in range(2 * RT):
                    i, half = n // 2, n % 2
                    cols = ACC[:, i, half * HALF:(half + 1) * HALF]
                    dve.wait_ge(d_full, f * 16 + (n + 1))
                    dve.tensor_tensor(cols, cols, PSM[:, 4 + n % 2, :], ALU.add).then_inc(d_free, 1)

            row_maximum(0)
            dve.wait_ge(misc_st, 16 * 4)
            dve.wait_ge(bank6_zero, 1)
            head_maximum(0)
            dve.memset(rden[:], 0.0).then_inc(d_free, 2)
            gate_times_up(0)
            hidden_lo(0, 0)
            dve.wait_ge(n1_alpha, RT)

            def iteration(i, last):
                for k in range(9):
                    r, s = k // 3, k % 3
                    f = i * 3 + (1 + r)
                    if k == 0:
                        subtract_maximum(i)
                    elif k == 1:
                        sum_probabilities(i)
                    elif k == 2:
                        invert_denominator(i)
                    if s == 1:
                        gate_times_up(f)
                    if s == 2:
                        hidden_lo(f, (1 + r) % 3)
                        if k == 8:
                            row_maximum(i + 1)
                            own_heads(i)
                        add_down(f - 1)
                    if k == 0:
                        dve.wait_ge(m_sub, i * 2 + 2)
                    if k < NCH:
                        reduce_keys(k, i * NCH + (NCH + k + 1))
                keep_columns(i)
                head_maximum(i + 1)

            LINKS = 5
            with dve.Fori(0, NITER - 1) as i:
                link.iteration(i, LINKS)
                iteration(i, False)
            link.after(NITER - 1)
            iteration(NITER - 1, True)
            subtract_maximum(NITER)
            sum_probabilities(NITER)
            add_down(FT - 1)
            invert_denominator(NITER)

            dve.wait_ge(d_free, FT * 16 + 2)
            for s in range(RT + 2):
                if s < RT:
                    statistics(s, P, ACC[:, s, :], n2_var)
                if 1 <= s <= RT:
                    v = s - 1
                    dve.wait_ge(n2_sd, v + 1)
                    inverse(v, P, n2_rs)
                if s >= 2:
                    v = s - 2
                    dve.wait_ge(n2_y, v + 1)
                    dve.wait_ge(ln2_ld, 32)
                    dve.tensor_tensor(ACC[:, v, :], ACC[:, v, :], LG2, ALU.mult).then_inc(n2_g, 1)
            own_heads(NITER)
            keep_columns(NITER)

            def sample_norm(residual, out, n, vectors, done, product):
                link(dve.scalar_tensor_tensor(out=xs2, in0=residual, scalar=ALPHA, in1=product,
                                              op0=ALU.mult, op1=ALU.add))
                statistics(RT, NB, xs2, e_var)
                dve.wait_ge(e_sd, n)
                inverse(RT, NB, e_rs)
                dve.wait_ge(e_rs, n)
                link(dve.tensor_scalar(xs2, xs2, rs[0:NB, RT, 0:1], rs[0:NB, RT, 1:2], ALU.mult, ALU.add))
                dve.wait_ge(*vectors)
                link(dve.tensor_tensor(xs2, xs2, sg, ALU.mult))
                dve.tensor_tensor(out, xs2, sbeta, ALU.add).then_inc(done, 1)

            mix = PSM[0:NB, 0:2, :].rearrange("p a n -> p (a n)")
            dve.wait_ge(e_ld, 48)
            dve.wait_ge(t_used, KC)
            sample_norm(xs1, xs1, 1, (e_ld, 48), e_x1, mix)
            dve.wait_ge(e_t, 1)
            dve.tensor_copy(CS[:].rearrange("p k b -> p (k b)"), PSM[:, 2, 0:KC * NB]).then_inc(e_xt, 1)

            with dve.Fori(0, FT // 2) as i:
                for r in range(2):
                    dve.wait_ge(e_silu, i * 2 + (r + 1))
                    if r == 0:
                        dve.wait_ge(t_used, i * 6 + KC)
                    dve.tensor_tensor(hid[:, r, :], hsilu[:, r, :], PSM[:, 4 + r, NB:2 * NB], ALU.mult).then_inc(e_hid, 1)
            dve.wait_ge(t_used, KC + 3 * FT)
            sample_norm(xs1, xs2, 2, (e_vec_ld, 32), e_y, mix)


def kernel(x_prompt, x_sample, cache_k, cache_v, cache_logf, state_pool, page_table, w_in, b_f, w_pool, pool_scale,
           w_o, ln1_g, ln1_b, w_gate, w_up, w_down, ln2_g, ln2_b):
    import concourse.bacc as bacc
    from concourse.bass_utils import run_bass_kernel_spmd

    def chunked(a):
        return a.reshape(KC, P, -1).transpose(1, 0, 2)

    def tiles(a, width):
        c = chunked(a)
        return c.reshape(P, KC, -1, width).transpose(2, 0, 1, 3).reshape(-1, P, KC * width)

    arr = {name: np.asarray(a) for name, a in locals().items() if name in (
        "x_prompt", "x_sample", "cache_k", "cache_v", "cache_logf", "state_pool", "page_table", "w_in", "b_f", "w_pool",
        "pool_scale", "w_o", "ln1_g", "ln1_b", "w_gate", "w_up", "w_down", "ln2_g", "ln2_b")}
    x, xs, win = arr["x_prompt"][0], arr["x_sample"][:, 0], arr["w_in"][0]
    q, k, v = (win[:, n * AW:(n + 1) * AW] for n in range(3))
    wf, u = win[:, 3 * AW:3 * AW + H], win[:, 3 * AW + H:]
    pair_order = np.concatenate([m[:, p * P:(p + 1) * P] for p in range(PAIRS) for m in (q, k, v)] + [u], axis=1)
    table = arr["page_table"].reshape(-1)

    row = np.arange(P)
    blkmask = np.zeros((P, H), np.float32)
    for j in range(4):
        for h in range(H):
            blkmask[32 * j + h, h] = 1
    cum = ((row[:, None] // NPAGE == row[None, :] // NPAGE) & (row[:, None] >= row[None, :])).astype(np.float32)
    scanmask = np.ones((P, H, P), np.float32)
    scanmask[:, :, 0] = 0
    rcnt = np.zeros((P, GROUPS, 16), np.float32)
    sel = np.zeros((NB, STATE, GROUPS, NB), np.float32)
    for g in range(GROUPS):
        w = 2 ** (g + 1)
        rcnt[:, g] = 1.0 / np.minimum(np.arange(16) + 1, w)
        for b in range(NB):
            sel[b, STATE - (w - 1):, g, b] = 1
    newmask = np.where(np.eye(NB, dtype=bool)[:, :, None], 0, NEG) * np.ones((1, 1, H))

    ins = {
        "xT": chunked(x.T), "xsT": chunked(xs.T).reshape(P, -1), "x": x, "xs": xs,
        "w_in": tiles(pair_order, P), "wf": chunked(wf).reshape(P, -1), "bf": arr["b_f"].reshape(H, 1),
        "w_pool": arr["w_pool"][0].transpose(1, 0, 2), "pscale": arr["pool_scale"].reshape(GROUPS, P).T,
        "w_o": arr["w_o"][0], "w_o4": tiles(arr["w_o"][0], OCW),
        "ffn": np.stack([tiles(arr["w_gate"][0], P), tiles(arr["w_up"][0], P), arr["w_down"][0].reshape(FT, P, D)], axis=1),
        "cache_k": arr["cache_k"].reshape(POOL_PAGES, P, AW), "cache_v": arr["cache_v"].reshape(POOL_PAGES, P, AW),
        "logf": arr["cache_logf"][0].transpose(0, 2, 1).reshape(POOL_PAGES, H * P),
        "state": arr["state_pool"].reshape(NB * STATE, AW),
        "page": table.reshape(1, -1), "page_row": table.reshape(2, P).T,
        "ln1_g": arr["ln1_g"], "ln1_b": arr["ln1_b"], "ln2_g": arr["ln2_g"], "ln2_b": arr["ln2_b"],
        "ident": np.eye(P, dtype=np.float32),
        "causal": np.where(row[None, :] <= row[:, None], 0, NEG).astype(np.float32),
        "blkmask": blkmask, "cum": cum, "scanmask": scanmask.reshape(P, -1), "rcnt": rcnt,
        "sel": sel.reshape(NB * STATE, GROUPS, NB), "newmask": newmask.astype(np.float32),
    }
    outs = {"y_p": (ROWS, D), "y_s": (NB, D), "k_p": (ROWS, AW), "v_p": (ROWS, AW), "f_p": (ROWS, H), "p_p": (STATE, AW),
            "k_s": (NB, AW), "v_s": (NB, AW), "f_s": (NB, H), "p_s": (NB, STATE, AW)}

    nc = bacc.Bacc("TRN2", target_bir_lowering=False, num_devices=1)
    arrays = {name: np.ascontiguousarray(a) for name, a in ins.items()}
    t = {name: nc.dram_tensor(name, a.shape, mybir.dt.from_np(a.dtype), kind="ExternalInput").ap()
         for name, a in arrays.items()}
    for name, shape in outs.items():
        t[name] = nc.dram_tensor(name, shape, F32, kind="ExternalOutput").ap()
    t["state3"] = t["state"].rearrange("(b s) n -> b s n", s=STATE)
    build(nc, t)
    r = run_bass_kernel_spmd(nc, [arrays], core_ids=[0]).results[0]
    return (r["y_p"].reshape(1, ROWS, D), r["y_s"].reshape(NB, 1, D),
            r["k_p"].reshape(1, 1, ROWS, H, HD), r["v_p"].reshape(1, 1, ROWS, H, HD), r["f_p"].reshape(1, 1, ROWS, H),
            r["p_p"].reshape(1, 1, STATE, AW), r["k_s"].reshape(1, NB, 1, H, HD), r["v_s"].reshape(1, NB, 1, H, HD),
            r["f_s"].reshape(1, NB, 1, H), r["p_s"].reshape(1, NB, STATE, AW))
```
